# Optimizing a Trainium2 kernel written in Bass

```python
import jax, jax.numpy as jnp
from jax import lax
import numpy as np

D_MODEL = 1024
BATCH = 1
SEQ = 1024
DEPTH = 2

CTX_LEN = 256
GRID_W = 64
HEAD_DIM = 64
A_Q_HEADS = 8
A_KV_HEADS = 2
A_GROUP = A_Q_HEADS // A_KV_HEADS
WINDOW = 128
ATTN_BLOCK = 128
ROPE_BASE = 10000.0
GLA_HEADS = 4
GLA_DK = 64
GLA_DV = 128
GLA_RANK = 16
GLA_TAU = 16.0
GLA_CHUNK = 64
A_Q_W = A_Q_HEADS * HEAD_DIM
A_KV_W = A_KV_HEADS * HEAD_DIM
GLA_K_W = GLA_HEADS * GLA_DK
GLA_V_W = GLA_HEADS * GLA_DV
EVEN_SPLITS = (A_Q_W, A_KV_W, A_KV_W, GLA_K_W, GLA_K_W, GLA_V_W, GLA_V_W, 2 * GLA_RANK)
EVEN_IN = sum(EVEN_SPLITS)
MIX_W = A_Q_W + GLA_V_W
CONV_W = 3
N_GROUPS = 4
EXPERTS_PER_GROUP = 8
N_EXPERTS = N_GROUPS * EXPERTS_PER_GROUP
TOP_K = 2
D_EXPERT = 512
MOE_BLOCK = 128
N_EVEN = (DEPTH + 1) // 2
N_ODD = DEPTH // 2
DEEPNORM_ALPHA = (2.0 * DEPTH) ** 0.25
DEEPNORM_BETA = (8.0 * DEPTH) ** -0.25
LN_EPS = 1e-5
RMS_EPS = 1e-6

kernel_name = 'hybrid_dit_swa_gla_shortconv_hmoe'

def layer_norm(x, w, b):
    xf = x.astype(jnp.float32)
    mu = jnp.mean(xf, -1, keepdims=True)
    var = jnp.mean(jnp.square(xf - mu), -1, keepdims=True)
    return ((xf - mu) * lax.rsqrt(var + LN_EPS) * w.astype(jnp.float32) + b.astype(jnp.float32)).astype(x.dtype)

def post_norm(x, y, w, b):
    return layer_norm(DEEPNORM_ALPHA * x + y, w, b)

def ada_modulation(cond, w, b):
    m = jax.nn.silu(cond) @ w + b
    return m.reshape(m.shape[:-1] + (6, D_MODEL))

def modulate(x, shift, scale):
    return x * (1 + scale) + shift

def axial_rope_tables(n_tok):
    n_rows = n_tok // GRID_W
    row = jnp.repeat(jnp.arange(n_rows), GRID_W).astype(jnp.float32)
    col = jnp.tile(jnp.arange(GRID_W), n_rows).astype(jnp.float32)
    axis_dim = HEAD_DIM // 2
    inv_freq = ROPE_BASE ** (-jnp.arange(0, axis_dim, 2, dtype=jnp.float32) / axis_dim)
    ang = jnp.concatenate([row[:, None] * inv_freq, col[:, None] * inv_freq], -1)
    return jnp.cos(ang), jnp.sin(ang)

def apply_rope(x, cos, sin):
    nf = HEAD_DIM // 4
    xs = x.astype(jnp.float32).reshape(x.shape[:-1] + (2, 2, nf))
    x1, x2 = xs[..., 0, :], xs[..., 1, :]
    c = cos.reshape(cos.shape[0], 1, 2, nf)
    s = sin.reshape(sin.shape[0], 1, 2, nf)
    out = jnp.stack([x1 * c - x2 * s, x2 * c + x1 * s], axis=-2)
    return out.reshape(x.shape).astype(x.dtype)

def split_even(p):
    idx = [sum(EVEN_SPLITS[:n]) for n in range(1, len(EVEN_SPLITS))]
    return jnp.split(p, idx, axis=-1)

def sink_attend(qg, k, v, sink, mask):
    s = jnp.einsum('bqgrd,bkgd->bgrqk', qg, k, preferred_element_type=jnp.float32) * (HEAD_DIM ** -0.5)
    if mask is not None:
        s = jnp.where(mask, s, -jnp.inf)
    s_sink = jnp.broadcast_to(sink.astype(jnp.float32).reshape(1, A_KV_HEADS, A_GROUP, 1, 1), s.shape[:-1] + (1,))
    p = jax.nn.softmax(jnp.concatenate([s, s_sink], -1), axis=-1)[..., :-1]
    return jnp.einsum('bgrqk,bkgd->bqgrd', p.astype(v.dtype), v)

def window_attention(q, k, v, k_ctx, v_ctx, sink):
    B, S = q.shape[:2]
    L = k_ctx.shape[1]
    nb = S // ATTN_BLOCK
    qb = q.reshape(B, nb, ATTN_BLOCK, A_KV_HEADS, A_GROUP, HEAD_DIM).transpose(1, 0, 2, 3, 4, 5)
    pad = ((0, 0), (ATTN_BLOCK, ATTN_BLOCK), (0, 0), (0, 0))

    def band(t):
        tp = jnp.pad(t, pad).reshape(B, nb + 2, ATTN_BLOCK, A_KV_HEADS, HEAD_DIM)
        return jnp.concatenate([tp[:, :-2], tp[:, 1:-1], tp[:, 2:]], axis=2).transpose(1, 0, 2, 3, 4)

    kwin, vwin = band(k), band(v)
    blk = jnp.arange(nb)[:, None] * ATTN_BLOCK
    q_pos = blk + jnp.arange(ATTN_BLOCK)[None]
    k_pos = blk - ATTN_BLOCK + jnp.arange(3 * ATTN_BLOCK)[None]
    band_mask = ((jnp.abs(q_pos[:, :, None] - k_pos[:, None, :]) <= WINDOW)
                 & (k_pos[:, None, :] >= 0) & (k_pos[:, None, :] < S))
    ctx_mask = jnp.ones((ATTN_BLOCK, L), bool)

    def one_block(args):
        qi, ki, vi, mi = args
        keys = jnp.concatenate([ki, k_ctx], axis=1)
        vals = jnp.concatenate([vi, v_ctx], axis=1)
        return sink_attend(qi, keys, vals, sink, jnp.concatenate([mi, ctx_mask], -1))

    o = lax.map(one_block, (qb, kwin, vwin, band_mask))
    return o.transpose(1, 0, 2, 3, 4, 5).reshape(B, S, A_Q_W)

def gla_inputs(q, k, v, g_lr, wa2_d, ba_d, d):
    B, T = q.shape[:2]
    g = g_lr[..., d * GLA_RANK:(d + 1) * GLA_RANK] @ wa2_d + ba_d
    log_a = jax.nn.log_sigmoid(g.astype(jnp.float32)) / GLA_TAU
    shp = (B, T, GLA_HEADS, -1)
    return [q.reshape(shp).astype(jnp.float32) * (GLA_DK ** -0.5), k.reshape(shp).astype(jnp.float32),
            v.reshape(shp).astype(jnp.float32), log_a.reshape(shp)]

def gla_chunked(q, k, v, log_a, s0):
    B, T, H, _ = q.shape
    dv = v.shape[-1]
    n = T // GLA_CHUNK

    def chunks(t):
        return t.reshape(B, n, GLA_CHUNK, H, t.shape[-1]).transpose(1, 0, 2, 3, 4)

    qc, kc, vc, ac = chunks(q), chunks(k), chunks(v), chunks(log_a)
    b = jnp.cumsum(ac, axis=2)
    b_last = b[:, :, -1:]
    q_in = qc * jnp.exp(b)
    k_in = kc * jnp.exp(-b)
    k_st = kc * jnp.exp(b_last - b)
    causal = jnp.tril(jnp.ones((GLA_CHUNK, GLA_CHUNK), bool))
    attn = jnp.where(causal, jnp.einsum('nbihd,nbjhd->nbhij', q_in, k_in), 0.0)
    o_intra = jnp.einsum('nbhij,nbjhv->nbihv', attn, vc)

    def step(s, xs):
        qi, ksi, vi, dl = xs
        o_inter = jnp.einsum('bihd,bhdv->bihv', qi, s)
        s = dl[:, 0, :, :, None] * s + jnp.einsum('bjhd,bjhv->bhdv', ksi, vi)
        return s, o_inter

    s_fin, o_inter = lax.scan(step, s0, (q_in, k_st, vc, jnp.exp(b_last)))
    o = (o_intra + o_inter).transpose(1, 0, 2, 3, 4).reshape(B, T, H, dv)
    return o, s_fin

def gla_final_state(k, v, log_a):
    b = jnp.cumsum(log_a, axis=1)
    return jnp.einsum('bthd,bthv->bhdv', k * jnp.exp(b[:, -1:] - b), v)

def gla_bidirectional(lat, ctx, wa2, ba, need_ctx):
    B = lat[0].shape[0]
    s0 = jnp.zeros((B, GLA_HEADS, GLA_DK, GLA_DV), jnp.float32)
    o_lat, o_ctx = 0.0, 0.0
    for d in range(2):
        lat_in = gla_inputs(*lat, wa2[d], ba[d], d)
        ctx_in = gla_inputs(*ctx, wa2[d], ba[d], d)
        if d == 1:
            lat_in = [jnp.flip(t, 1) for t in lat_in]
            ctx_in = [jnp.flip(t, 1) for t in ctx_in]
        if need_ctx:
            oc, s_ctx = gla_chunked(*ctx_in, s0)
            o_ctx = o_ctx + (jnp.flip(oc, 1) if d == 1 else oc)
        else:
            s_ctx = gla_final_state(*ctx_in[1:])
        ol, _ = gla_chunked(*lat_in, s_ctx)
        o_lat = o_lat + (jnp.flip(ol, 1) if d == 1 else ol)
    return o_lat, o_ctx

def gla_output(o, r, norm_w):
    o = o * lax.rsqrt(jnp.mean(jnp.square(o), -1, keepdims=True) + RMS_EPS)
    o = o.reshape(o.shape[:2] + (GLA_V_W,)).astype(r.dtype) * norm_w
    return o * jax.nn.silu(r)

def attn_gla_mixer(u_lat, u_ctx, cos, sin, w_in, w_out, sink, wa2, ba, norm_w, need_ctx):
    B, S, _ = u_lat.shape
    L = u_ctx.shape[1]
    qa, ka, va, qg, kg, vg, rg, gg = split_even(u_lat @ w_in)
    qa_c, ka_c, va_c, qg_c, kg_c, vg_c, rg_c, gg_c = split_even(u_ctx @ w_in)

    def heads(t, h):
        return t.reshape(t.shape[:2] + (h, HEAD_DIM))

    k_ctx, v_ctx = heads(ka_c, A_KV_HEADS), heads(va_c, A_KV_HEADS)
    a_lat = window_attention(apply_rope(heads(qa, A_Q_HEADS), cos, sin), apply_rope(heads(ka, A_KV_HEADS), cos, sin),
                             heads(va, A_KV_HEADS), k_ctx, v_ctx, sink)
    o_lat, o_ctx = gla_bidirectional((qg, kg, vg, gg), (qg_c, kg_c, vg_c, gg_c), wa2, ba, need_ctx)
    y_lat = jnp.concatenate([a_lat, gla_output(o_lat, rg, norm_w)], -1) @ w_out
    if not need_ctx:
        return y_lat, None
    qc = qa_c.reshape(B, L, A_KV_HEADS, A_GROUP, HEAD_DIM)
    a_ctx = sink_attend(qc, k_ctx, v_ctx, sink, None).reshape(B, L, A_Q_W)
    y_ctx = jnp.concatenate([a_ctx, gla_output(o_ctx, rg_c, norm_w)], -1) @ w_out
    return y_lat, y_ctx

def short_conv_mixer(h, w_in, conv_w, conv_b, w_out):
    gb, gc, u = jnp.split(h @ w_in, 3, axis=-1)
    up = jnp.pad(gc * u, ((0, 0), (1, 1), (0, 0)))
    y = up[:, :-2] * conv_w[0] + up[:, 1:-1] * conv_w[1] + up[:, 2:] * conv_w[2] + conv_b
    return (gb * y) @ w_out

def routed_expert_ffn(h, expert, weights, w1, w3, w2):
    N, D = h.shape
    A = N * TOP_K
    flat_e = expert.reshape(A)
    flat_tok = jnp.repeat(jnp.arange(N), TOP_K)
    flat_w = weights.reshape(A)
    order = jnp.argsort(flat_e)
    e_sorted, tok_sorted, w_sorted = flat_e[order], flat_tok[order], flat_w[order]
    counts = jnp.bincount(flat_e, length=N_EXPERTS)
    start = jnp.cumsum(counts) - counts
    padded = (counts + MOE_BLOCK - 1) // MOE_BLOCK * MOE_BLOCK
    pad_end = jnp.cumsum(padded)
    pad_start = pad_end - padded
    dest = pad_start[e_sorted] + jnp.arange(A) - start[e_sorted]
    n_blocks = -(-A // MOE_BLOCK) + N_EXPERTS
    buf = jnp.zeros((n_blocks * MOE_BLOCK, D), h.dtype).at[dest].set(h[tok_sorted])
    blk_expert = jnp.minimum(jnp.searchsorted(pad_end, jnp.arange(n_blocks) * MOE_BLOCK, side='right'), N_EXPERTS - 1)

    def expert_block(args):
        xb, e = args
        return (jax.nn.silu(xb @ w1[e]) * (xb @ w3[e])) @ w2[e]

    y = lax.map(expert_block, (buf.reshape(n_blocks, MOE_BLOCK, D), blk_expert)).reshape(-1, D)
    return jnp.zeros((N, D), h.dtype).at[tok_sorted].add(y[dest] * w_sorted[:, None].astype(h.dtype))

def hier_moe(h, wg, bg, we, be, w1, w3, w2):
    N = h.shape[0]
    hf = h.astype(jnp.float32)
    g_logits = hf @ wg.astype(jnp.float32) + bg.astype(jnp.float32)
    _, g_sel = lax.top_k(g_logits, 1)
    p_group = jnp.take_along_axis(jax.nn.softmax(g_logits, -1), g_sel, -1)
    e_logits = (hf @ we.astype(jnp.float32) + be.astype(jnp.float32)).reshape(N, N_GROUPS, EXPERTS_PER_GROUP)
    e_logits = jnp.take_along_axis(e_logits, g_sel[:, :, None], 1)[:, 0]
    top_p, top_i = lax.top_k(jax.nn.softmax(e_logits, -1), TOP_K)
    weights = p_group * top_p / jnp.sum(top_p, -1, keepdims=True)
    expert = g_sel * EXPERTS_PER_GROUP + top_i
    return routed_expert_ffn(h, expert, weights, w1, w3, w2)

def setup_inputs(seed: int = 0) -> dict:
    key = jax.random.key(seed)
    ks = jax.random.split(key, 25)
    D = D_MODEL

    def nrm(k, shape, s):
        return jax.random.normal(k, shape, jnp.float32) * s

    return {
        'x': nrm(ks[0], (BATCH, SEQ, D), 1.0),
        'c': nrm(ks[1], (BATCH, D), 1.0),
        'ctx': nrm(ks[2], (BATCH, CTX_LEN, D), 1.0),
        'c_ctx': nrm(ks[3], (D,), 1.0),
        'w_in_even': nrm(ks[4], (N_EVEN, D, EVEN_IN), D ** -0.5),
        'w_out_even': nrm(ks[5], (N_EVEN, MIX_W, D), MIX_W ** -0.5 * DEEPNORM_BETA),
        'attn_sink': nrm(ks[6], (N_EVEN, A_Q_HEADS), 1.0),
        'gla_wa2': nrm(ks[7], (N_EVEN, 2, GLA_RANK, GLA_K_W), GLA_RANK ** -0.5),
        'gla_ba': nrm(ks[8], (N_EVEN, 2, GLA_K_W), 0.1),
        'gla_norm_w': 1.0 + nrm(ks[9], (N_EVEN, GLA_V_W), 0.02),
        'w_in_odd': nrm(ks[10], (N_ODD, D, 3 * D), D ** -0.5),
        'conv_w': nrm(ks[11], (N_ODD, CONV_W, D), CONV_W ** -0.5),
        'conv_b': nrm(ks[12], (N_ODD, D), 0.02),
        'w_out_odd': nrm(ks[13], (N_ODD, D, D), D ** -0.5 * DEEPNORM_BETA),
        'ada_w': nrm(ks[14], (DEPTH, D, 6 * D), 0.5 * D ** -0.5),
        'ada_b': nrm(ks[15], (DEPTH, 6 * D), 0.02),
        'ln_w': 1.0 + nrm(ks[16], (DEPTH, 2, D), 0.02),
        'ln_b': nrm(ks[17], (DEPTH, 2, D), 0.02),
        'router_wg': nrm(ks[18], (DEPTH, D, N_GROUPS), D ** -0.5),
        'router_bg': nrm(ks[19], (DEPTH, N_GROUPS), 0.01),
        'router_we': nrm(ks[20], (DEPTH, D, N_EXPERTS), D ** -0.5),
        'router_be': nrm(ks[21], (DEPTH, N_EXPERTS), 0.01),
        'moe_w1': nrm(ks[22], (DEPTH, N_EXPERTS, D, D_EXPERT), D ** -0.5),
        'moe_w3': nrm(ks[23], (DEPTH, N_EXPERTS, D, D_EXPERT), D ** -0.5),
        'moe_w2': nrm(ks[24], (DEPTH, N_EXPERTS, D_EXPERT, D), D_EXPERT ** -0.5 * DEEPNORM_BETA),
    }

def reference(x, c, ctx, c_ctx, w_in_even, w_out_even, attn_sink, gla_wa2, gla_ba, gla_norm_w,
              w_in_odd, conv_w, conv_b, w_out_odd, ada_w, ada_b, ln_w, ln_b,
              router_wg, router_bg, router_we, router_be, moe_w1, moe_w3, moe_w2):
    B, S, D = x.shape
    L = ctx.shape[1]
    cos, sin = axial_rope_tables(S)
    h_lat, h_ctx = x, ctx
    for l in range(DEPTH):
        i = l // 2
        need_ctx = any(j % 2 == 0 for j in range(l + 1, DEPTH))
        mod = ada_modulation(c, ada_w[l], ada_b[l])
        m = [mod[:, n, None] for n in range(6)]
        u_lat = modulate(h_lat, m[0], m[1])
        if need_ctx or l % 2 == 0:
            mc = ada_modulation(c_ctx, ada_w[l], ada_b[l])
            u_ctx = modulate(h_ctx, mc[0], mc[1])
        if l % 2 == 0:
            y_lat, y_ctx = attn_gla_mixer(u_lat, u_ctx, cos, sin, w_in_even[i], w_out_even[i], attn_sink[i],
                                          gla_wa2[i], gla_ba[i], gla_norm_w[i], need_ctx)
        else:
            y_lat = short_conv_mixer(u_lat, w_in_odd[i], conv_w[i], conv_b[i], w_out_odd[i])
            y_ctx = short_conv_mixer(u_ctx, w_in_odd[i], conv_w[i], conv_b[i], w_out_odd[i]) if need_ctx else None
        h_lat = post_norm(h_lat, m[2] * y_lat, ln_w[l, 0], ln_b[l, 0])
        tokens = modulate(h_lat, m[3], m[4]).reshape(B * S, D)
        if need_ctx:
            h_ctx = post_norm(h_ctx, mc[2] * y_ctx, ln_w[l, 0], ln_b[l, 0])
            tokens = jnp.concatenate([tokens, modulate(h_ctx, mc[3], mc[4]).reshape(B * L, D)], 0)
        y = hier_moe(tokens, router_wg[l], router_bg[l], router_we[l], router_be[l], moe_w1[l], moe_w3[l], moe_w2[l])
        h_lat = post_norm(h_lat, m[5] * y[:B * S].reshape(B, S, D), ln_w[l, 1], ln_b[l, 1])
        if need_ctx:
            h_ctx = post_norm(h_ctx, mc[5] * y[B * S:].reshape(B, L, D), ln_w[l, 1], ln_b[l, 1])
    return h_lat


_drawn_inputs = setup_inputs


def setup_inputs(seed=0):
    import zlib

    import numpy as np

    out = dict(_drawn_inputs(seed))
    spreads = {}
    factors = {'ctx': 7.578,
     'c_ctx': 4.34,
     'attn_sink': 64.0,
     'gla_wa2': 6.463,
     'gla_ba': 8.0,
     'gla_norm_w': 64.0,
     'conv_b': 21.867,
     'ada_b': 3.816,
     'router_bg': 58.212,
     'router_be': 56.04}
    for name, (base, spread) in spreads.items():
        noise = np.random.default_rng([zlib.crc32(name.encode()), seed]).standard_normal(out[name].shape)
        drawn = base * np.exp(spread * noise) if base else spread * noise
        out[name] = __import__('jax').numpy.asarray(drawn.astype(out[name].dtype))
    for name, factor in factors.items():
        out[name] = (out[name] * factor).astype(out[name].dtype)
    return out
```

```python
from contextlib import ExitStack

import numpy as np
import concourse.bass as bass
from concourse import mybir

D, SEQ, CTX, DEPTH = 1024, 1024, 256, 2
P = 128
NT, NTC = SEQ // P, (SEQ + CTX) // P
KC = D // P
EVEN_IN = 2336
Q0, K0, V0, GQ0, GK0, GV0, R0, G0 = 0, 512, 640, 768, 1024, 1280, 1792, 2304
HEADS, HD = 8, 64
GH, DV = 4, 128
NE, NG, DE = 32, 4, 512
OVER = 15
TABLE = NE + OVER + 4
ROWS = 2 * SEQ
ALPHA = (2.0 * DEPTH) ** 0.25
LN_EPS, RMS_EPS = 1e-5, 1e-6
NEG = -1e30

C_LAYOUT = [("ident", P), ("tri0", P), ("tri1", P), ("rest0", P), ("rest1", P), ("causal0", P), ("causal1", P),
            ("strict", P), ("ones", P), ("chunk", 2), ("cos", NT * 32), ("sin", NT * 32), ("mask", 3 * 640),
            ("rank4", NG), ("rank32", NE), ("first", NE), ("over", NE), ("slot", 16 * NE)]
C_AT, _n = {}, 0
for _name, _w in C_LAYOUT:
    C_AT[_name] = (_n, _n + _w)
    _n += _w
C_W = _n


def constants():
    c = np.zeros((P, C_W), np.float32)

    def put(name, a):
        lo, hi = C_AT[name]
        c[:, lo:hi] = a

    i = np.arange(P)
    same = (i[:, None] // 64) == (i[None, :] // 64)
    put("ident", np.eye(P))
    put("tri0", (same & (i[:, None] <= i[None, :])) / 16.0)
    put("tri1", (same & (i[:, None] >= i[None, :])) / 16.0)
    put("rest0", (same & (i[:, None] > i[None, :])) / 16.0)
    put("rest1", (same & (i[:, None] < i[None, :])) / 16.0)
    put("causal0", same & (i[:, None] <= i[None, :]))
    put("causal1", same & (i[:, None] >= i[None, :]))
    put("strict", i[:, None] < i[None, :])
    put("ones", 1.0)
    put("chunk", (i[:, None] // 64 == np.arange(2)[None]) / 16.0)
    t = np.arange(SEQ)
    inv = (10000.0 ** (-np.arange(0, 32, 2, dtype=np.float32) / np.float32(32))).astype(np.float32)
    ang = np.concatenate([(t // 64).astype(np.float32)[:, None] * inv, (t % 64).astype(np.float32)[:, None] * inv], -1)
    put("cos", np.cos(ang).reshape(NT, P, 32).transpose(1, 0, 2).reshape(P, -1))
    put("sin", np.sin(ang).reshape(NT, P, 32).transpose(1, 0, 2).reshape(P, -1))
    j = np.arange(384)
    near = (j[None] >= i[:, None]) & (j[None] <= i[:, None] + 256)
    m = np.zeros((P, 3, 640), np.float32)
    for n, ok in enumerate((near & (j[None] >= 128), near, near & (j[None] < 256))):
        m[:, n, :384] = np.where(ok, 0.0, NEG)
    put("mask", m.reshape(P, -1))
    put("rank4", NG - np.arange(NG))
    put("rank32", NE - np.arange(NE))
    put("first", P * np.arange(NE))
    put("over", P * NE - P - P * np.arange(NE))
    put("slot", np.repeat(np.arange(16), NE))
    return c


def row_numbers():
    p, k, t = np.meshgrid(np.arange(P), np.arange(2), np.arange(NT), indexing="ij")
    return (2 * (t * P + p) + k).reshape(P, 16).astype(np.int32)


def program(nc, T, out):
    f32, i32 = mybir.dt.float32, mybir.dt.int32
    ALU, ACT, AX = mybir.AluOpType, mybir.ActivationFunctionType, mybir.AxisListType
    MUL, ADD, SUB, MAX, MIN = ALU.mult, ALU.add, ALU.subtract, ALU.max, ALU.min

    ctx = ExitStack()
    with ctx:
        sems = {}

        def S(name):
            if name not in sems:
                sems[name] = ctx.enter_context(nc.semaphore(name))
            return sems[name]

        def sb(name, shape, dt=f32):
            return ctx.enter_context(nc.sbuf_tensor(name, shape, dt))

        def hold(eng):
            eng.sem_inc(S(f"held_{eng.engine}"), 1)

        class Steps:

            def __init__(self, eng, name):
                self.eng, self.sem, self.n = eng, S(name), 0

            def __call__(self, ins):
                ins.then_inc(self.sem, 1)
                self.n = self.n + 1

            def wait(self):
                self.eng.wait_ge(self.sem, self.n)

        bigA = sb("bigA", [P, 24576])
        bigB = sb("bigB", [P, 10240])
        bigC = sb("bigC", [P, 8192])
        cst = sb("cst", [P, C_W])
        gate = sb("gate", [P, 2, D])
        lnwb = sb("lnwb", [P, 2 * D])
        lnw, lnb = lnwb[:, 0:D], lnwb[:, D:]
        wa2x = sb("wa2x", [33, 512])
        normw = sb("normw", [P, GH * DV])
        states = lnwb[:, :].rearrange("p (s n r v) -> p s n r v", s=2, n=4, r=2)
        small = sb("small", [P, 512])
        ints = sb("ints", [P, 160], i32)
        banks = [ctx.enter_context(nc.psum_tensor(f"bank{b}", [P, 1024], f32)) for b in range(4)]

        def bank(b, n=1):
            return banks[b // 2][:, (b % 2) * 512:(b % 2 + n) * 512]

        def cc(name):
            lo, hi = C_AT[name]
            return cst[:, lo:hi]

        ident = cc("ident")

        def at(big, off, *shape):
            n = int(np.prod(shape))
            v = big[:, off:off + n]
            if len(shape) == 1:
                return v
            names = "abcd"[:len(shape)]
            return v.rearrange(f"p ({' '.join(names)}) -> p {' '.join(names)}", **dict(zip(names[1:], shape[1:])))

        def wide(ap, shape):
            return ap.to_broadcast(shape)

        smoff = [0]

        def col(n):
            smoff[0] += n
            assert smoff[0] <= 512
            return small[:, smoff[0] - n:smoff[0]]

        cond = col(16).rearrange("p (k s) -> p k s", s=2)
        craw = col(16).rearrange("p (s k) -> p s k", s=2)
        condx = col(16).rearrange("p (s k) -> p s k", s=2)
        modc = col(64).rearrange("p (m k s) -> p m k s", m=4, k=KC)
        sink = col(8)
        mx, nmx, rden = (col(8) for _ in range(3))
        rsum = col(16).rearrange("p (j h) -> p j h", j=2)
        dlx = col(8).rearrange("p (s r) -> p s r", s=2)
        ms = col(32)
        rms = col(32)
        bn6 = col(24).rearrange("p (j s) -> p j s", j=2)
        mv = col(4).rearrange("p (j s) -> p j s", j=2)
        sd, rs, nm = (col(2) for _ in range(3))
        wts = col(16).rearrange("p (k t) -> p k t", k=2)
        convp = col(32).rearrange("p (m c) -> p m c", m=4)
        epsc = col(2)
        rownum, dest, tok = ints[:, 0:16], ints[:, 16:32], ints[:, 32:32 + TABLE]
        rows_of = ints[:, 32 + TABLE:32 + 2 * TABLE]
        gidx = ints[:, 134:136]
        sidx = ints[:, 136:138]
        ov = ints[:, 138:155]

        h_dram = [nc.dram_tensor(f"h_rows{l}", [SEQ, D], f32, kind="Internal").ap() for l in range(DEPTH)]
        y_dram = [nc.dram_tensor(f"y_rows{l}", [ROWS, D], f32, kind="Internal").ap() for l in range(DEPTH)]
        t_dram = [nc.dram_tensor(f"table{l}", [TABLE * P, 1], i32, kind="Internal").ap() for l in range(DEPTH)]

        proj = at(bigA, 0, NTC, EVEN_IN)
        uT = at(bigB, 0, KC, NTC * P)
        wring = at(bigC, 0, 2, KC, 512)
        mrows = at(bigA, 0, 4, D)
        mrows1 = at(bigA, 5120, 4, D)
        condb = at(bigA, 4096, KC, P)
        xring = at(bigA, 6144, 3, D)
        adab = at(bigA, 12288, 6 * D)
        kinT = at(bigA, 23360, 2, 2, P)
        gates_log = at(bigB, 0, NTC, 512)
        kT = at(bigB, 5120, 1536)
        lowT = at(bigB, 6656, NTC, P)
        expo = at(bigB, 7936, 2, 3, 256)
        logs = at(bigB, 9472, 2, 256)
        mix = at(bigC, 0, NT, D)
        hh = mix
        qzT = [mix[:, s, 0:512].rearrange("p (h i) -> p h i", h=GH) for s in range(2)]
        amat = [mix[:, 2 + s, 0:512].rearrange("p (h i) -> p h i", h=GH) for s in range(2)]
        kst = [mix[:, 4 + s, 0:512].rearrange("p (c d) -> p c d", c=2) for s in range(2)]
        qkin = [mix[:, 6 + s, 0:512].rearrange("p (a d) -> p a d", a=2) for s in range(2)]
        qrow = at(bigB, 0, 2, 512)
        qz = at(bigB, 1024, 2, HEADS, P)
        sc = at(bigB, 3072, 2, 642)
        pr = [at(bigB, 4356, 642), at(bigB, 6656, 642)]
        prT = at(bigB, 7298, 2, 640)
        wout = at(bigA, 0, KC, D)
        mixT = at(bigA, 8192, 2, KC, P)
        zt = at(bigA, 10240, 2, D)
        xin = at(bigA, 12288, 2, D)
        w13 = [[at(bigA, 12288 * s + 4096 * m, KC, DE) for m in range(2)] for s in range(2)]
        w2 = [at(bigA, 12288 * s + 8192, DE // P, D) for s in range(2)]
        xg = at(bigB, 0, 2, D)
        xT = at(bigB, 2048, 2, KC, P)
        yo = at(bigB, 4096, 2, D)
        sg, gg = at(bigB, 6656, DE), at(bigB, 7168, DE)
        gT = at(bigB, 7680, DE // P, P)
        wr = at(bigB, 8192, KC, NG + NE)
        rbias = at(bigB, 8480, NG + NE)
        route = bigB[:, 8704:10240]
        pair = at(bigA, 0, 2, 2, D)
        rope_tmp = at(bigC, 0, 4, 320)
        gate_min = at(bigC, 1280, 2, 512)
        gate_abs = at(bigC, 2304, 2, 512)
        glo_tmp = at(bigB, 0, 2, 512)
        squares = at(bigB, 1024, NT, GH, DV)
        ada1 = at(bigA, 14336, 2, KC, 512)
        adab1 = at(bigB, 0, 6 * D)
        zt1 = at(bigA, 16384, 2, D)
        chosen = route[:, 0:256]
        logit = route[:, 256:544].rearrange("p (t n) -> p t n", t=NT)
        pick = route[:, 544:1056].rearrange("p (k t e) -> p k t e", k=2, t=NT)
        rt = [at(bigB, 4096 + 256 * n, NT, NE) for n in range(8)]
        rs8 = [at(bigB, 6144 + 32 * n, NT, NG) for n in range(4)]
        rc8 = [bigB[:, 6400 + 8 * n:6408 + 8 * n] for n in range(12)]
        re32 = [bigB[:, 6528 + 32 * n:6560 + 32 * n] for n in range(6)]
        rov = at(bigB, 7168, 16, NE)
        u1T = at(bigB, 0, KC, SEQ)
        wc = at(bigA, 0, 2, 3, KC, P)
        zT = at(bigA, 8192, KC, SEQ)
        conv_in = at(bigA, 16384, 2, SEQ + 2)
        conv_b2 = at(bigA, 16384 + 2056, 2, SEQ)
        conv_u = at(bigA, 16384 + 2056 + 2048, 2, 512)
        conv_y = at(bigA, 16384 + 2056 + 2048 + 1024, SEQ)
        wout1 = at(bigB, 0, KC, D)

        block = ctx.enter_context(nc.Block())

        def state_at(s, c, q):
            return 2 * q + (c if s == 0 else 1 - c)

        def run_gla(eng, step):
            step(0, None, 0, (NT, NT + 1), False)
            step(1, None, 1, (NT + 1, NT), False)
            for half in range(2):
                with eng.Fori(0, NT // 4) as i:
                    for q in range(2):
                        m = 2 * i + (q + half * NT // 2)
                        step(m + 2, m, q, (m, i * -2 + (NT - 1 - q - half * NT // 2)), half == 1)

        def run_att(eng, block_):
            block_(0, 0, 0)
            with eng.Fori(0, NT // 2 - 1) as i:
                for j in range(2):
                    block_(2 * i + 1 + j, 1 - j, 1)
            block_(NT - 1, (NT - 1) % 2, 2)

        def run_blocks(eng, l, hidden, product, block_):
            hidden(0, 0, False)
            with eng.Fori(0, NE // 2 - 1) as i:
                hidden(i, 1, True)
                hidden(i + 1, 0, True)
            hidden(NE // 2 - 1, 1, True)
            product(NE // 2 - 1, 1)
            run_over(eng, l, block_)

        def run_over(eng, l, block_):
            eng.wait_ge(S("routed"), l + 1)
            n_over = eng.value_load(ov[0:1, 16:17], min_val=0, max_val=OVER)
            with eng.Fori(0, 8) as i:
                for j in range(2):
                    with eng.If(2 * i + j < n_over):
                        block_(i + NE // 2, j)

        groups = [(0, 512), (512, 512), (1024, 512), (1536, 512), (2048, 288)]
        units = [(g, t) for g in range(5) for t in range(NTC) if t < NT or g]
        last_unit = {g: max(n for n, u in enumerate(units) if u[0] == g) for g in range(5)}

        def cols(ap, n=KC):
            return ap.rearrange("p (q k) -> p k q", k=n)

        @block.sync
        def _(sp):
            def load(dst, src, name, **how):
                sp.dma_start(dst, src, **how).then_inc(S(name), 16)

            load(cst[:, :], T["const_f"], "const_in")
            load(craw[:, 0, :], T["c"].rearrange("o (p k) -> (o p) k", k=KC), "cond_in")
            load(craw[:, 1, :], T["c_ctx"].rearrange("(p k) -> p k", k=KC), "cond_in")
            load(rownum, T["const_i"], "cond_in")
            sp.wait_ge(S("wa2_zero"), 1)
            load(wa2x[0:16, 0:256], T["gla_wa2"][0, 0], "wa2_in")
            load(wa2x[16:32, 256:512], T["gla_wa2"][0, 1], "wa2_in")
            load(wa2x[32:33, :], T["gla_ba"][0].rearrange("(o d) n -> o (d n)", o=1), "wa2_in")
            load(sink, T["attn_sink"][0:1, :].to_broadcast([P, HEADS]), "wa2_in")
            load(normw[:, :], T["gla_norm_w"][0:1, :].to_broadcast([P, GH * DV]), "wa2_in")
            for m in range(3):
                load(convp[:, m, :], T["conv_w"][0, m].rearrange("(c p) -> p c", p=P), "wa2_in",
                     allow_slow_non_contiguous=True)
            load(convp[:, 3, :], T["conv_b"][0].rearrange("(c p) -> p c", p=P), "wa2_in",
                     allow_slow_non_contiguous=True)
            for l in range(DEPTH):
                load(t_dram[l], T["const_t"], "cond_in")

            def ada_chunk(l, n):
                if n >= 2:
                    sp.wait_ge(S("ada_mm"), l * 12 + n - 1)
                load((wring, ada1)[l][:, n % 2],
                     T["ada_w"][l].rearrange("(p k) n -> p k n", k=KC)[:, :, n * 512:(n + 1) * 512], f"ada_in{n % 2}")

            def ada(l):
                load((adab, adab1)[l][0:1, :], T["ada_b"][l:l + 1, :], "adab_in")
                for n in range(12):
                    ada_chunk(l, n)

            def ln_params(l, j):
                load(lnw, T["ln_w"][l, j:j + 1, :].to_broadcast([P, D]), "ln_in")
                load(lnb, T["ln_b"][l, j:j + 1, :].to_broadcast([P, D]), "ln_in")

            ada(0)
            for t in range(NTC):
                if t >= 3:
                    sp.wait_ge(S("tile_T"), t - 2)
                src = T["x"][0, t * P:(t + 1) * P, :] if t < NT else T["ctx"][0, (t - NT) * P:(t - NT + 1) * P, :]
                load(xring[:, t % 3], src, f"x_in{t % 3}")
            sp.wait_ge(S("ada_mm"), 12)
            for g, (lo, w) in enumerate(groups):
                if g >= 2:
                    sp.wait_ge(S("proj_mm"), last_unit[g - 2] + 1)
                load(wring[:, g % 2, :, 0:w], T["w_in_even"][0].rearrange("(p k) n -> p k n", k=KC)[:, :, lo:lo + w],
                     f"w_in{g % 2}")
            sp.wait_ge(S("att_out"), NT)
            ln_params(0, 0)
            load(wout, T["w_out_even"][0].rearrange("(p k) n -> p k n", k=KC), "wout_in0")
            for t in range(NT):
                if t >= 2:
                    sp.wait_ge(S("res"), t - 1)
                load(xin[:, t % 2], T["x"][0, t * P:(t + 1) * P, :], f"x_in{t % 2}")
            for l in range(DEPTH):
                for t in range(NT):
                    sp.wait_ge(S("ln"), 2 * l * NT + t + 1)
                    sp.dma_start(h_dram[l][t * P:(t + 1) * P, :], hh[:, t]).then_inc(S("h_out"), 16)
                ln_params(l, 1)
                load(wr[:, :, 0:NG], T["router_wg"][l].rearrange("(p k) n -> p k n", k=KC), "wr_in")
                load(wr[:, :, NG:], T["router_we"][l].rearrange("(p k) n -> p k n", k=KC), "wr_in")
                load(rbias[0:1, 0:NG], T["router_bg"][l:l + 1, :], "wr_in")
                load(rbias[0:1, NG:], T["router_be"][l:l + 1, :], "wr_in")

                def load_w13(e, j):
                    for m, n in enumerate(("moe_w1", "moe_w3")):
                        src = T[n][l].rearrange("e (p k) n -> p e (k n)", k=KC)
                        load(w13[j][m].rearrange("p k n -> p (k n)"), src[:, bass.ds(e, 1), :].squeeze(1), f"w13_in{l}_{j}")

                def load_w2(e, j):
                    src = T["moe_w2"][l].rearrange("e (p k) n -> p e (k n)", k=DE // P)
                    load(w2[j].rearrange("p k n -> p (k n)"), src[:, bass.ds(e, 1), :].squeeze(1), f"w2_in{l}_{j}")

                for j in range(2):
                    load_w13(j, j)
                    load_w2(j, j)

                def next_weights(b, j):
                    sp.wait_ge(S(f"h_mm{l}"), 2 * b + 2)
                    load_w13(b + 2, j)
                    sp.wait_ge(S(f"y_mm{l}"), b)
                    load_w2(b + 1, 1 - j)

                sp.wait_ge(S(f"h_mm{l}"), 2)
                load_w13(2, 0)
                with sp.Fori(0, NE // 2 - 2) as i:
                    next_weights(2 * i + 1, 1)
                    next_weights(2 * i + 2, 0)
                next_weights(NE - 3, 1)
                sp.wait_ge(S(f"y_mm{l}"), NE - 2)
                load_w2(NE - 1, 1)
                sp.wait_ge(S("routed"), l + 1)
                n_over = sp.value_load(ov[0:1, 16:17], min_val=0, max_val=OVER)
                with sp.Fori(0, 8) as i:
                    for j in range(2):
                        o = 2 * i + j
                        with sp.If(o < n_over):
                            e = sp.value_load(ov[0:1, bass.ds(o, 1)], min_val=0, max_val=NE - 1)
                            sp.wait_ge(S(f"h_mm{l}"), 2 * (o + NE - 1))
                            load_w13(e, j)
                            sp.wait_ge(S(f"y_mm{l}"), o + NE - 1)
                            load_w2(e, j)
                sp.wait_ge(S("rows_out"), l + 1)
                for t in range(NT):
                    if t >= 2:
                        sp.wait_ge(S("comb"), l * NT + t - 1)
                    load(pair[:, t % 2], y_dram[l][t * 2 * P:(t + 1) * 2 * P, :].rearrange("(p k) n -> p k n", k=2),
                         f"pair_in{t % 2}")
                    if l == 0:
                        if t == 1:
                            load(adab1[0:1, :], T["ada_b"][1:2, :], "adab_in")
                            ada_chunk(1, 0)
                        if t:
                            ada_chunk(1, t)
                if l == DEPTH - 1:
                    for t in range(NT):
                        sp.wait_ge(S("ln"), (2 * l + 1) * NT + t + 1)
                        sp.dma_start(out[0, t * P:(t + 1) * P, :], hh[:, t]).then_inc(S("out_done"), 16)
                    sp.wait_ge(S("out_done"), 16 * NT)
                    return
                for n in range(NT, 12):
                    ada_chunk(1, n)
                sp.wait_ge(S("ln"), 2 * NT)
                ln_params(1, 0)
                sp.wait_ge(S("modc_mm"), 2)
                w_odd = T["w_in_odd"][0].rearrange("(p k) (m c n) -> p m k c n", k=KC, m=3, n=P)
                for c in range(2):
                    for m in range(3):
                        load(wc[:, c, m], w_odd[:, m, :, c, :], f"wc_in{c}")
                with sp.Fori(0, NT // 2 - 1) as i:
                    for j in range(2):
                        c = 2 * i + j
                        sp.wait_ge(S("conv_mm"), 2 * c + 2)
                        for m in range(3):
                            load(wc[:, j, m], w_odd[:, m, :, bass.ds(c + 2, 1), :].squeeze(2), f"wc_in{j}")
                sp.wait_ge(S("conv_mm"), 16)
                load(wout1, T["w_out_odd"][0].rearrange("(k p) n -> p k n", p=P), "wout_in1")

        @block.tensor
        def _(pe):
            mm, tp = nc.tensor.matmul, nc.tensor.transpose

            def ada(l):
                pe.wait_ge(S("adab_in"), l * 16 + 16)
                if l == 0:
                    pe.wait_ge(S("const_in"), 16)
                pe.wait_ge(S("cond_ok"), l + 1)
                ring = wring if l == 0 else ada1
                for n in range(12):
                    m = n // 2
                    pe.wait_ge(S(f"ada_in{n % 2}"), 16 * (6 * l + n // 2 + 1))
                    if n >= 2:
                        pe.wait_ge(S("ada_ev"), l * 12 + n - 1)
                    M = P if m in (2, 5) else 2
                    dst = bank(n % 2)[0:M, :]
                    mm(dst, cc("ones")[0:1, 0:M], (adab, adab1)[l][0:1, n * 512:(n + 1) * 512], start=True, stop=False)
                    for k in range(KC):
                        lhs = condb[:, k, :] if M == P else cond[:, k, :]
                        last = mm(dst, lhs, ring[:, n % 2, k, :], start=False, stop=(k == KC - 1))
                    last.then_inc(S("ada_mm"), 1)
                pe.wait_ge(S("ada_ev"), l * 12 + 12)
                for m in range(4):
                    for k in range(KC):
                        last = mm(bank(2)[:, (m * KC + k) * 2:(m * KC + k) * 2 + 2], cols((mrows, mrows1)[l][0:2, m])[:, k, :],
                                  ident[0:2, 0:2], start=True, stop=True)
                last.then_inc(S("modc_mm"), 1)

            def transposes(src, b, n=KC):
                for k in range(n):
                    last = tp(bank(b + k // 4)[:, (k % 4) * P:(k % 4 + 1) * P], cols(src, n)[:, k, :], ident)
                return last

            ada(0)
            for t in range(NTC):
                pe.wait_ge(S(f"x_in{t % 3}"), 16 * (t // 3 + 1))
                if t >= 2:
                    pe.wait_ge(S("tile_a"), t - 1)
                    pe.wait_ge(S("tile_d"), t - 1)
                transposes(xring[:, t % 3], 4 + 2 * (t % 2)).then_inc(S("tile_T"), 1)
            pe.wait_ge(S("tile_a"), NTC)
            pe.wait_ge(S("tile_d"), NTC)
            for n, (g, t) in enumerate(units):
                if n == 0 or units[n - 1][0] != g:
                    pe.wait_ge(S(f"w_in{g % 2}"), 16 * (g // 2 + 1))
                if n >= 4:
                    pe.wait_ge(S("proj_a" if n % 2 == 0 else "proj_d"), (n - 4) // 2 + 1)
                w = groups[g][1]
                for k in range(KC):
                    last = mm(bank(n % 4)[:, 0:w], uT[:, k, t * P:(t + 1) * P], wring[:, g % 2, k, 0:w],
                              start=(k == 0), stop=(k == KC - 1))
                last.then_inc(S("proj_mm"), 1)
            pe.wait_ge(S("wa2_in"), 144)
            pe.wait_ge(S("proj_a"), len(units) // 2)
            pe.wait_ge(S("proj_d"), len(units) // 2)
            for t in range(NTC):
                if t < NT:
                    pe.wait_ge(S("rope"), t + 1)
                if t >= 1:
                    pe.wait_ge(S("low_ev"), t)
                tp(bank(4)[:, 0:P], proj[:, t, K0:K0 + P], ident)
                tp(bank(4)[0:32, P:2 * P], proj[:, t, G0:G0 + 32], ident).then_inc(S("low_T"), 1)
                pe.wait_ge(S("low_ev"), t + 1)
                if t == 0:
                    pe.wait_ge(S("k_pad"), 1)
                if t >= 2:
                    pe.wait_ge(S("gate_d"), t - 1)
                mm(bank(t % 2), lowT[0:33, t, :], wa2x[:, :], start=True, stop=True).then_inc(S("gate_mm"), 1)
            pe.wait_ge(S("gate_d"), NTC)

            def gla(n, m, q, ts, add):
                lat = m is not None
                for s in range(2):
                    b = 4 * s
                    pe.wait_ge(S("g_log"), 2 * n + s + 1)
                    pe.wait_ge(S("g_dl"), 2 * n)
                    if lat:
                        pe.wait_ge(S("g_oe"), 2 * m + 2)
                        mm(bank(b)[:, 0:256], cc(f"tri{s}"), logs[:, s, :], start=True, stop=True)
                    mm(bank(b)[:, 256:512], cc(f"rest{s}"), logs[:, s, :], start=True, stop=True)
                    for r in range(2):
                        last = mm(bank(b + 1)[:, 2 * r:2 * r + 2], logs[:, s, r * P:(r + 1) * P], cc("chunk"),
                                  start=True, stop=True)
                    last.then_inc(S("g_cum"), 1)
                if lat:
                    for s in range(2):
                        b = 4 * s
                        pe.wait_ge(S("g_qk"), 2 * m + s + 1)
                        pe.wait_ge(S("g_dl"), 2 * n + s + 1)
                        for a in range(2):
                            for r in range(2):
                                last = tp(bank(b + 1)[:, (2 * a + r) * P:(2 * a + r + 1) * P],
                                          qkin[s][:, a, r * P:(r + 1) * P], ident)
                        last.then_inc(S("g_T"), 1)
                for s in range(2):
                    b = 4 * s
                    pe.wait_ge(S("g_kst"), 2 * n + s + 1)
                    pe.wait_ge(S("g_st"), 2 * n)
                    for c in range(2):
                        for r in range(2):
                            last = mm(bank(b + 2 + c)[:, r * 256:(r + 1) * 256], kst[s][:, c, r * P:(r + 1) * P],
                                      proj[:, ts[s], GV0 + r * 256:GV0 + (r + 1) * 256], start=True, stop=True)
                    last.then_inc(S("g_u"), 1)
                if not lat:
                    return
                for s in range(2):
                    b = 4 * s
                    pe.wait_ge(S("g_eva"), 2 * m + s + 1)
                    pe.wait_ge(S("g_evd"), 2 * m + s + 1)
                    for r in range(2):
                        last = mm(bank(b)[:, r * 256:(r + 1) * 256], kinT[:, s, r, :],
                                  qzT[s][:, 2 * r:2 * r + 2, :].rearrange("p h i -> p (h i)"), start=True, stop=True)
                    last.then_inc(S("g_a"), 1)
                for s in range(2):
                    b = 4 * s
                    pe.wait_ge(S("g_am"), 2 * m + s + 1)
                    pe.wait_ge(S("g_st"), 2 * n + s + 1)
                    for h in range(GH):
                        mm(bank(b + 1)[:, h * DV:(h + 1) * DV], amat[s][:, h, :],
                           proj[:, ts[s], GV0 + h * DV:GV0 + (h + 1) * DV], start=True, stop=False,
                           skip_group_check=True)
                        for c in range(2):
                            last = mm(bank(b + 1)[c * 64:(c + 1) * 64, h * DV:(h + 1) * DV],
                                      qzT[s][:, h, c * 64:(c + 1) * 64], states[:, s, state_at(s, c, q), h // 2, :],
                                      start=False, stop=(c == 1), skip_group_check=True)
                    last.then_inc(S("g_o"), 1)

            run_gla(pe, gla)

            for s in range(2):
                pe.wait_ge(S("g_oe"), 2 * NT + 2)
                pe.wait_ge(S("g_st"), 2 * NT + 4)

            def attend(n, j, edge):
                pe.wait_ge(S("q_row"), n + 1)
                pe.wait_ge(S("q_ev_a"), n)
                pe.wait_ge(S("q_ev_d"), n)
                for r in range(4):
                    last = tp(bank(6)[:, r * P:(r + 1) * P], qrow[:, j, r * P:(r + 1) * P], ident)
                last.then_inc(S("q_T"), 1)
                pe.wait_ge(S("q_ev_a"), n + 1)
                pe.wait_ge(S("q_ev_d"), n + 1)

                def scores(h):
                    if edge or h:
                        pe.wait_ge(S("sc_d"), 8 * n + h - 1)
                    dst = banks[h % 2]
                    q = qz[:, j, h, :]
                    mm(dst[:, 0:384], q, kT[:, bass.ds(n * P, 384)], start=True, stop=True)
                    mm(dst[:, 384:512], q, kT[:, 1280:1408], start=True, stop=True, skip_group_check=True)
                    mm(dst[:, 512:640], q, kT[:, 1408:1536], start=True, stop=True).then_inc(S("sc_mm"), 1)

                scores(0)
                for h in range(HEADS):
                    if h + 1 < HEADS:
                        scores(h + 1)
                    pe.wait_ge(S("p_a"), 8 * n + h + 1)
                    pe.wait_ge(S("pT_a"), 8 * n + h)
                    pe.wait_ge(S("pT_d"), 8 * n + h)
                    for k in range(5):
                        last = tp(bank(4 + k // 2 - k // 4)[:, (k - 2 * (k > 1)) * P:(k - 2 * (k > 1) + 1) * P], pr[h % 2][:, k * P:(k + 1) * P], ident)
                    last.then_inc(S("p_T"), 1)
                    pe.wait_ge(S("pT_a"), 8 * n + h + 1)
                    pe.wait_ge(S("pT_d"), 8 * n + h + 1)
                    if h == 0:
                        pe.wait_ge(S("att_out"), n)
                    g = h // 4
                    ks = [k for k in range(5) if not (edge == 0 and k == 0) and not (edge == 2 and k == 2)]
                    for k in ks:
                        if k < 3:
                            v = proj[:, n - 1 + k, V0 + g * HD:V0 + (g + 1) * HD]
                        else:
                            v = proj[:, NT + k - 3, V0 + g * HD:V0 + (g + 1) * HD]
                        last = mm(bank(7)[:, h * HD:(h + 1) * HD], prT[:, h % 2, k * P:(k + 1) * P], v,
                                  start=(k == ks[0]), stop=(k == 4))
                    last.then_inc(S("pv_mm"), 1)

            pe.wait_ge(S("k_pad"), 3)
            pe.wait_ge(S("qz_zero"), 4)
            run_att(pe, attend)

            pe.wait_ge(S("sc_d"), 8 * NT)
            pe.wait_ge(S("pT_a"), 8 * NT)
            pe.wait_ge(S("pT_d"), 8 * NT)
            pe.wait_ge(S("att_out"), NT)

            def out_product(l, lhs_of, w):
                for t in range(NT):
                    lhs = lhs_of(t)
                    if t >= 2:
                        pe.wait_ge(S("res"), l * NT + t - 1)
                    for n in range(2):
                        for k in range(KC):
                            last = mm(bank(2 * (t % 2) + n), lhs(k), w[:, k, n * 512:(n + 1) * 512], start=(k == 0),
                                      stop=(k == KC - 1))
                    last.then_inc(S("out_mm"), 1)

            def mixT_of(t):
                if t == 0:
                    pe.wait_ge(S("gla_done"), 1)
                    pe.wait_ge(S("wout_in0"), 16)
                if t >= 2:
                    pe.wait_ge(S("tile_a"), NTC + t - 1)
                    pe.wait_ge(S("tile_d"), NTC + t - 1)
                transposes(mix[:, t], 4 + 2 * (t % 2)).then_inc(S("tile_T"), 1)
                pe.wait_ge(S("tile_a"), NTC + t + 1)
                pe.wait_ge(S("tile_d"), NTC + t + 1)
                return lambda k: mixT[:, t % 2, k, :]

            def moe(l):
                pe.wait_ge(S("wr_in"), l * 64 + 64)
                for t in range(NT):
                    pe.wait_ge(S("ln"), 2 * l * NT + t + 1)
                    if t >= 2:
                        pe.wait_ge(S("tile_a"), NTC + NT + 2 * NT * l + t - 1)
                        pe.wait_ge(S("tile_d"), NTC + NT + 2 * NT * l + t - 1)
                    transposes(hh[:, t], 4 + 2 * (t % 2)).then_inc(S("tile_T"), 1)
                    pe.wait_ge(S("tile_a"), NTC + NT + 2 * NT * l + t + 1)
                    pe.wait_ge(S("tile_d"), NTC + NT + 2 * NT * l + t + 1)
                    dst = bank(0)[:, t * 36:(t + 1) * 36]
                    mm(dst, cc("ones")[0:1, :], rbias[0:1, :], start=True, stop=False)
                    for k in range(KC):
                        last = mm(dst, xT[:, t % 2, k, :], wr[:, k, :], start=False, stop=(k == KC - 1))
                last.then_inc(S("logits"), 1)
                pe.wait_ge(S("chosen"), l + 1)
                rank = bank(2)[:, 0:NT * NE]
                mm(rank, cc("strict"), chosen, start=True, stop=False, skip_group_check=True)
                for t in range(NT - 1):
                    src = chosen[:, t * NE:(t + 1) * NE].unsqueeze(1)
                    mm(rank[:, (t + 1) * NE:].rearrange("p (t e) -> p t e", e=NE), cc("ones"),
                       wide(src, [P, NT - 1 - t, NE]), start=False, stop=(t == NT - 2), skip_group_check=True)
                for t in range(NT):
                    last = mm(bank(3)[:, 0:NE], cc("ones"), chosen[:, t * NE:(t + 1) * NE], start=(t == 0),
                              stop=(t == NT - 1))
                last.then_inc(S("ranked"), 1)

                def rows_T(i, j):
                    b = 2 * i + j
                    pe.wait_ge(S(f"xg_in{l}_{j}"), 16 * (i + 1))
                    transposes(xg[:, j], 2).then_inc(S(f"x_T{l}"), 1)

                def hidden_half(i, j, m):
                    b = 2 * i + j
                    if m == 0:
                        pe.wait_ge(S(f"xT_a{l}"), b + 1)
                        pe.wait_ge(S(f"xT_d{l}"), b + 1)
                        pe.wait_ge(S(f"silu_a{l}"), b + 1)
                        pe.wait_ge(S(f"w13_in{l}_{j}"), 32 * (i + 1))
                    for k in range(KC):
                        last = mm(bank(m), xT[:, j, k, :], w13[j][m][:, k, :], start=(k == 0), stop=(k == KC - 1))
                    last.then_inc(S(f"h_mm{l}"), 1)

                def gated_T(b):
                    pe.wait_ge(S(f"g_d{l}"), b + 2)
                    for k in range(DE // P):
                        last = tp(bank(4 + k // 2)[:, (k % 2) * P:(k % 2 + 1) * P], cols(gg, DE // P)[:, k, :], ident)
                    last.then_inc(S(f"g_T{l}"), 1)

                def output(i, j):
                    b = 2 * i + j
                    pe.wait_ge(S(f"gT_a{l}"), b + 1)
                    pe.wait_ge(S(f"gT_d{l}"), b + 1)
                    pe.wait_ge(S(f"y_a{l}"), b + 1)
                    pe.wait_ge(S(f"y_d{l}"), b + 1)
                    pe.wait_ge(S(f"w2_in{l}_{j}"), 16 * (i + 1))
                    for n in range(2):
                        for k in range(DE // P):
                            last = mm(bank(6 + n), gT[:, k, :], w2[j][:, k, n * 512:(n + 1) * 512], start=(k == 0),
                                      stop=(k == DE // P - 1))
                    last.then_inc(S(f"y_mm{l}"), 1)

                def hidden(i, j, after):
                    b = 2 * i + j
                    hidden_half(i, j, 0)
                    if after:
                        gated_T(b - 1)
                    hidden_half(i, j, 1)
                    rows_T(i + j, 1 - j)
                    if after:
                        output(i + j - 1, 1 - j)

                def product(i, j):
                    gated_T(2 * i + j)
                    output(i, j)

                def block_of(i, j):
                    pe.wait_ge(S(f"g_d{l}"), 2 * i + j + 1)
                    hidden_half(i, j, 0)
                    hidden_half(i, j, 1)
                    rows_T(i + j, 1 - j)
                    product(i, j)

                rows_T(0, 0)
                run_blocks(pe, l, hidden, product, block_of)

            def conv_chunk(i, j):
                c = 2 * i + j
                pe.wait_ge(S(f"wc_in{j}"), 48 * (i + 1))
                for half in range(2):
                    pe.wait_ge(S("conv_a"), 2 * c + half + 1)
                    pe.wait_ge(S("conv_d"), 2 * c + half + 1)
                    for m in range(3):
                        for k in range(KC):
                            last = mm(bank(3 * half + m), wc[:, j, m, k, :], u1T[:, k, half * 512:(half + 1) * 512],
                                      start=(k == 0), stop=(k == KC - 1))
                    last.then_inc(S("conv_mm"), 1)

            out_product(0, mixT_of, wout)
            moe(0)
            ada(1)
            for t in range(NT):
                pe.wait_ge(S("ln"), NT + t + 1)
                if t >= 2:
                    pe.wait_ge(S("tile_a"), NTC + 2 * NT + t - 1)
                    pe.wait_ge(S("tile_d"), NTC + 2 * NT + t - 1)
                transposes(hh[:, t], 4 + 2 * (t % 2)).then_inc(S("tile_T"), 1)
            pe.wait_ge(S("tile_a"), NTC + 2 * NT + NT)
            pe.wait_ge(S("tile_d"), NTC + 2 * NT + NT)
            with pe.Fori(0, KC // 2) as i:
                for j in range(2):
                    conv_chunk(i, j)
            pe.wait_ge(S("z_ok"), KC + 2)
            pe.wait_ge(S("wout_in1"), 16)
            out_product(1, lambda t: (lambda k: zT[:, k, t * P:(t + 1) * P]), wout1)
            moe(1)

        @block.scalar
        def _(act):
            A = Steps(act, "act_step")
            go = nc.scalar.activation

            def ada_chunk(l, n):
                m, half = n // 2, (n % 2) * 512
                act.wait_ge(S("ada_mm"), l * 12 + n + 1)
                if l == 1 and n == 10:
                    act.wait_ge(S("comb"), NT)
                if m in (2, 5):
                    dst, src = gate[:, m // 3, half:half + 512], bank(n % 2)
                else:
                    dst, src = (mrows, mrows1)[l][0:2, {0: 0, 1: 1, 3: 2, 4: 3}[m], half:half + 512], bank(n % 2)[0:2, :]
                go(dst, src, ACT.Copy).then_inc(S("ada_ev"), 1)

            def ada(l):
                for n in range(12):
                    ada_chunk(l, n)
                act.wait_ge(S("modc"), l + 1)

            def modulated(dst, b, m, s, done):
                for k in range(4):
                    last = go(dst[:, k, :], bank(b)[:, k * P:(k + 1) * P], ACT.Identity, bias=modc[:, m, k, s:s + 1],
                              scale=modc[:, m + 1, k, s:s + 1])
                last.then_inc(S(done), 1)

            act.wait_ge(S("cond_in"), 80)
            go(condx, craw, ACT.Exp, scale=-1.0).then_inc(S("cond_e"), 1)
            ada(0)
            for t in range(NTC):
                act.wait_ge(S("tile_T"), t + 1)
                modulated(uT[:, :, t * P:(t + 1) * P], 4 + 2 * (t % 2), 0, int(t >= NT), "tile_a")
            for n, (g, t) in enumerate(units):
                if n % 2 == 0:
                    lo, w = groups[g]
                    act.wait_ge(S("proj_mm"), n + 1)
                    go(proj[:, t, lo:lo + w], bank(n % 4)[:, 0:w], ACT.Copy).then_inc(S("proj_a"), 1)
            act.wait_ge(S("proj_mm"), len(units))
            for t in range(NTC):
                act.wait_ge(S("low_T"), t + 1)
                off = (t + 1 if t < NT else t + 2) * P
                go(kT[:, off:off + P], bank(4)[:, 0:P], ACT.Copy)
                go(lowT[0:32, t, :], bank(4)[0:32, P:2 * P], ACT.Copy).then_inc(S("low_ev"), 1)
                act.wait_ge(S("gate_mm"), t + 1)
                if t >= 2:
                    act.wait_ge(S("gate_d"), t - 1)
                ga = gate_abs[:, t % 2]
                go(gate_min[:, t % 2], bank(t % 2), ACT.Copy)
                A(go(ga, bank(t % 2), ACT.Abs))
                A.wait()
                A(go(ga, ga, ACT.Exp, scale=-1.0))
                A.wait()
                go(ga, ga, ACT.Ln, bias=1.0).then_inc(S("gate_ln"), 1)

            def gla(n, m, q, ts, add):
                for s in range(2):
                    b = 4 * s
                    act.wait_ge(S("g_cum"), 2 * n + s + 1)
                    act.wait_ge(S("g_kst"), 2 * n)
                    act.wait_ge(S("g_st"), 2 * n)
                    if m is not None:
                        go(expo[:, s, 0, :], bank(b)[:, 0:256], ACT.Exp)
                        go(expo[:, s, 1, :], bank(b)[:, 0:256], ACT.Exp, scale=-1.0)
                    go(expo[:, s, 2, :], bank(b)[:, 256:512], ACT.Exp)
                    go(dlx[:, s, :], bank(b + 1)[:, 0:4], ACT.Exp).then_inc(S("g_dl"), 1)
                if m is not None:
                    for s in range(2):
                        act.wait_ge(S("g_evd"), 2 * m + s + 1)
                        go(kinT[:, s, :, :].rearrange("p r i -> p (r i)"), bank(4 * s + 1)[:, 256:512], ACT.Copy)\
                            .then_inc(S("g_eva"), 1)

            run_gla(act, gla)
            act.wait_ge(S("ms_ok"), 1)
            go(rms, ms, ACT.Sqrt, bias=epsc[:, 1:2], scale=1.0 / DV).then_inc(S("rms_a"), 1)
            for t in range(NT):
                if t >= 2:
                    act.wait_ge(S("glo_d"), t - 1)
                go(glo_tmp[:, t % 2], proj[:, t, R0:R0 + 512], ACT.Silu).then_inc(S("glo_a"), 1)

            def attend(n, j, edge):
                act.wait_ge(S("q_T"), n + 1)
                go(qz[0:64, j, 0:4, :].rearrange("p h i -> p (h i)"), bank(6)[0:64, :], ACT.Copy).then_inc(S("q_ev_a"), 1)
                for h in range(HEADS):
                    act.wait_ge(S("sc_d"), 8 * n + h + 1)
                    act.wait_ge(S("sink_c"), 8 * n + h + 1)
                    if edge or h:
                        act.wait_ge(S("p_T"), 8 * n + h - 1)
                    go(nmx[:, h:h + 1], mx[:, h:h + 1], ACT.Copy, scale=-1.0).then_inc(S("nmx_a"), 1)
                    act.wait_ge(S("nmx_a"), 8 * n + h + 1)
                    go(pr[h % 2][:, 0:641], sc[:, h % 2, 0:641], ACT.Exp, bias=nmx[:, h:h + 1],
                       accum_out=rsum[:, j, h:h + 1]).then_inc(S("p_a"), 1)
                    act.wait_ge(S("p_T"), 8 * n + h + 1)
                    go(prT[:, h % 2, 0:256], bank(4)[:, 0:256], ACT.Copy).then_inc(S("pT_a"), 1)

            run_att(act, attend)

            def ln(norm, t, z):
                j, n = t % 2, NT * norm + t
                act.wait_ge(S("var"), n + 1)
                go(sd[:, j:j + 1], mv[:, j, 1:2], ACT.Sqrt, bias=epsc[:, 0:1]).then_inc(S("sd"), 1)
                act.wait_ge(S("nmr"), n + 1)
                go(z[:, j], z[:, j], ACT.Identity, bias=nm[:, j:j + 1], scale=rs[:, j:j + 1]).then_inc(S("nrm"), 1)

            def moe(l):
                for t in range(NT):
                    act.wait_ge(S("tile_T"), NTC + NT + 2 * NT * l + t + 1)
                    modulated(xT[:, t % 2], 4 + 2 * (t % 2), 2, 0, "tile_a")
                act.wait_ge(S("gd_d"), l + 1)
                go(rs8[1], rs8[0], ACT.Exp).then_inc(S("route_a"), 1)
                act.wait_ge(S("dlt_d"), l + 1)
                go(rc8[6], rc8[5], ACT.Exp).then_inc(S("route_a"), 1)

                def rows_T(i, j):
                    b = 2 * i + j
                    act.wait_ge(S(f"x_T{l}"), b + 1)
                    modulated(xT[:, j], 2, 2, 0, f"xT_a{l}")

                def silu(b):
                    act.wait_ge(S(f"g_d{l}"), b + 1)
                    act.wait_ge(S(f"h_mm{l}"), 2 * b + 1)
                    go(sg, bank(0), ACT.Silu).then_inc(S(f"silu_a{l}"), 1)

                def gated(b):
                    act.wait_ge(S(f"g_T{l}"), b + 1)
                    go(gT[:, 0:2, :].rearrange("p k i -> p (k i)"), bank(4)[:, 0:256], ACT.Copy).then_inc(S(f"gT_a{l}"), 1)

                def output(b, j):
                    act.wait_ge(S(f"y_mm{l}"), b + 1)
                    act.wait_ge(S(f"yo_free{l}"), b + 1)
                    go(yo[:, j, 0:512], bank(6), ACT.Copy).then_inc(S(f"y_a{l}"), 1)

                def hidden(i, j, after):
                    b = 2 * i + j
                    silu(b)
                    if after:
                        gated(b - 1)
                    rows_T(i + j, 1 - j)
                    if after:
                        output(b - 1, 1 - j)

                def product(i, j):
                    gated(2 * i + j)
                    output(2 * i + j, j)

                def block_of(i, j):
                    silu(2 * i + j)
                    rows_T(i + j, 1 - j)
                    product(i, j)

                rows_T(0, 0)
                act.sem_inc(S(f"y_a{l}"), 1)
                act.sem_inc(S(f"silu_a{l}"), 1)
                run_blocks(act, l, hidden, product, block_of)

            for t in range(NT):
                act.wait_ge(S("tile_T"), NTC + t + 1)
                go(mixT[:, t % 2, 0:4, :].rearrange("p k i -> p (k i)"), bank(4 + 2 * (t % 2)), ACT.Copy)\
                    .then_inc(S("tile_a"), 1)
                if t:
                    ln(0, t - 1, zt)
            ln(0, NT - 1, zt)
            moe(0)
            for t in range(NT):
                ln(1, t, zt)
                ada_chunk(1, t)
            for n in range(NT, 12):
                ada_chunk(1, n)
            act.wait_ge(S("modc"), 2)
            for t in range(NT):
                act.wait_ge(S("tile_T"), NTC + 2 * NT + t + 1)
                modulated(u1T[:, :, t * P:(t + 1) * P], 4 + 2 * (t % 2), 0, 0, "tile_a")
            act.sem_inc(S("conv_a"), 2)
            with act.Fori(0, KC // 2) as i:
                for j in range(2):
                    c = 2 * i + j
                    for half in range(2):
                        act.wait_ge(S("conv_mm"), 2 * c + half + 1)
                        if half == 0:
                            act.wait_ge(S("z_ok"), c + 1)
                        go(conv_u[:, half], bank(3 * half + 1), ACT.Copy)
                        go(conv_b2[:, j, half * 512:(half + 1) * 512], bank(3 * half), ACT.Copy).then_inc(S("conv_a"), 1)
            for t in range(NT):
                ln(2, t, zt1)
            moe(1)
            for t in range(NT):
                ln(3, t, zt)

        @block.vector
        def _(dve):
            V = Steps(dve, "dve_step")
            v = nc.vector
            v.memset(wa2x[:, :], 0.0).then_inc(S("wa2_zero"), 1)
            v.memset(epsc[:, 0:1], LN_EPS)
            V(v.memset(epsc[:, 1:2], RMS_EPS))

            def modulated(dst, b, m, s, done):
                for k in range(4, KC):
                    last = v.tensor_scalar(dst[:, k, :], bank(b + 1)[:, (k - 4) * P:(k - 3) * P],
                                           modc[:, m + 1, k, s:s + 1], modc[:, m, k, s:s + 1], MUL, ADD)
                last.then_inc(S(done), 1)

            def cond_rows(l):
                for k in range(KC):
                    last = v.tensor_scalar(condb[:, k, :], cc("ones"), cond[:, k, 0:1], None, MUL)
                last.then_inc(S("cond_ok"), 1)

            def mod_columns(l):
                dve.wait_ge(S("modc_mm"), l + 1)
                for m in range(4):
                    src = bank(2)[:, m * 16:(m + 1) * 16].rearrange("p (k s) -> p k s", s=2)
                    if m % 2:
                        last = v.tensor_scalar(modc[:, m], src, 1.0, None, ADD)
                    else:
                        last = v.tensor_copy(modc[:, m], src)
                last.then_inc(S("modc"), 1)
                dve.wait_ge(S("modc"), l + 1)

            dve.wait_ge(S("cond_e"), 1)
            V(v.tensor_scalar(condx, condx, 1.0, None, ADD))
            V.wait()
            V(v.reciprocal(condx, condx))
            V.wait()
            V(v.tensor_tensor(cond.rearrange("p k s -> p s k"), craw, condx, MUL))
            V.wait()
            dve.wait_ge(S("const_in"), 16)
            cond_rows(0)
            mod_columns(0)
            for t in range(NTC):
                dve.wait_ge(S("tile_T"), t + 1)
                modulated(uT[:, :, t * P:(t + 1) * P], 4 + 2 * (t % 2), 0, int(t >= NT), "tile_d")
            for n, (g, t) in enumerate(units):
                if n % 2:
                    lo, w = groups[g]
                    dve.wait_ge(S("proj_mm"), n + 1)
                    v.tensor_copy(proj[:, t, lo:lo + w], bank(n % 4)[:, 0:w]).then_inc(S("proj_d"), 1)
            dve.wait_ge(S("proj_mm"), len(units))
            dve.wait_ge(S("proj_a"), len(units) // 2)
            dve.wait_ge(S("proj_d"), len(units) // 2)

            def rotate(t):
                x = proj[:, t, 0:640].rearrange("p (h a u f) -> p h a u f", a=2, u=2, f=16)
                x1, x2 = x[:, :, :, 0, :], x[:, :, :, 1, :]
                cs, sn = (wide(cc(n)[:, t * 32:(t + 1) * 32].rearrange("p (a f) -> p a f", a=2).unsqueeze(1),
                               [P, 10, 2, 16]) for n in ("cos", "sin"))
                dve.wait_ge(S("rope"), t)
                tmp = [rope_tmp[:, n].rearrange("p (h a f) -> p h a f", h=10, a=2) for n in range(4)]
                v.tensor_tensor(tmp[0], x1, cs, MUL)
                v.tensor_tensor(tmp[1], x2, sn, MUL)
                v.tensor_tensor(tmp[2], x2, cs, MUL)
                V(v.tensor_tensor(tmp[3], x1, sn, MUL))
                V.wait()
                v.tensor_tensor(x1, tmp[0], tmp[1], SUB)
                v.tensor_tensor(x2, tmp[2], tmp[3], ADD).then_inc(S("rope"), 1)

            def decay_min(t):
                dve.wait_ge(S("gate_ln"), t + 1)
                v.scalar_tensor_tensor(gates_log[:, t, :], gate_min[:, t % 2], 0.0, gate_abs[:, t % 2], MIN, SUB)\
                    .then_inc(S("gate_d"), 1)

            rotate(0)
            for t in range(NTC):
                if t + 1 < NT:
                    rotate(t + 1)
                decay_min(t)
            dve.wait_ge(S("gate_d"), NTC)
            for s in range(2):
                v.memset(qzT[s], 0.0)
                v.memset(amat[s], 0.0)
                v.memset(kst[s], 0.0)
                V(v.memset(states[:, s, 0], 0.0))
            V.wait()

            def gla(n, m, q, ts, add):
                lat = m is not None
                for s in range(2):
                    t = ts[s]
                    dve.wait_ge(S("g_dl"), 2 * n + s + 1)
                    if lat:
                        v.scalar_tensor_tensor(qkin[s][:, 0, :], proj[:, t, GQ0:GQ0 + 256], GLA_SCALE,
                                               expo[:, s, 0, :], MUL, MUL)
                        v.tensor_tensor(qkin[s][:, 1, :], proj[:, t, GK0:GK0 + 256], expo[:, s, 1, :], MUL)\
                            .then_inc(S("g_qk"), 1)
                    for c in range(2):
                        rows = slice(c * 64, (c + 1) * 64)
                        last = v.tensor_tensor(kst[s][rows, c, :], proj[rows, t, GK0:GK0 + 256], expo[rows, s, 2, :], MUL)
                    last.then_inc(S("g_kst"), 1)
                if lat:
                    for s in range(2):
                        dve.wait_ge(S("g_T"), 2 * m + s + 1)
                        for u in range(2):
                            rows = slice(u * 64, (u + 1) * 64)
                            last = v.tensor_copy(qzT[s].rearrange("p (r u) i -> p r u i", u=2)[rows, :, u, :],
                                                 bank(4 * s + 1)[rows, 0:256].rearrange("p (r i) -> p r i", r=2))
                        last.then_inc(S("g_evd"), 1)
                for f in range(2):
                    for s in range(2):
                        c = f if s == 0 else 1 - f
                        if f == 0:
                            dve.wait_ge(S("g_u"), 2 * n + s + 1)
                            dve.wait_ge(S("g_st"), 2 * n)
                        else:
                            dve.wait_ge(S("g_mid"), 2 * n + s + 1)
                        src, dst = 2 * q + f, (2 * q + 1, 2 * (1 - q))[f]
                        for r in range(2):
                            for u in range(2):
                                rows = slice(u * 64, (u + 1) * 64)
                                last = v.scalar_tensor_tensor(
                                    states[rows, s, dst, r, :], states[rows, s, src, r, :], dlx[rows, s, 2 * r + c:2 * r + c + 1],
                                    bank(4 * s + 2 + c)[rows, r * 256 + u * DV:r * 256 + (u + 1) * DV], MUL, ADD)
                        last.then_inc(S("g_st" if f else "g_mid"), 1)
                if not lat:
                    return
                for s in range(2):
                    dve.wait_ge(S("g_a"), 2 * m + s + 1)
                    hold(v)
                    mask = wide(cc(f"causal{s}").bitcast(i32).unsqueeze(1), [P, GH, P])
                    v.copy_predicated(amat[s], mask, bank(4 * s).rearrange("p (h i) -> p h i", h=GH))\
                        .then_inc(S("g_am"), 1)
                for s in range(2):
                    dve.wait_ge(S("g_o"), 2 * m + s + 1)
                    dst = mix[:, ts[s], 512:1024]
                    if add:
                        dve.wait_ge(S("g_oe"), NT + 2)
                        v.tensor_tensor(dst, dst, bank(4 * s + 1), ADD).then_inc(S("g_oe"), 1)
                    else:
                        v.tensor_copy(dst, bank(4 * s + 1)).then_inc(S("g_oe"), 1)

            v.sem_inc(S("g_oe"), 2)
            run_gla(dve, gla)
            for s in range(2):
                dve.wait_ge(S("g_oe"), 2 * NT + 2)
                dve.wait_ge(S("g_st"), 2 * NT + 4)
            for t in range(NT):
                for h in range(GH):
                    o = mix[:, t, 512 + h * DV:512 + (h + 1) * DV]
                    last = v.tensor_tensor_reduce(out=squares[:, t, h], in0=o, in1=o, scale=1.0, scalar=0.0, op0=MUL,
                                                  op1=ADD, accum_out=ms[:, t * GH + h:t * GH + h + 1])
            last.then_inc(S("ms_ok"), 1)
            dve.wait_ge(S("rms_a"), 1)
            V(v.reciprocal(rms, rms))
            V.wait()
            for t in range(NT):
                j = t % 2
                o = mix[:, t, 512:1024]
                oh = o.rearrange("p (h d) -> p h d", h=GH)
                dve.wait_ge(S("glo_a"), t + 1)
                V(v.tensor_tensor(oh, oh, wide(rms[:, t * GH:(t + 1) * GH].unsqueeze(2), [P, GH, DV]), MUL))
                V.wait()
                V(v.tensor_tensor(o, o, normw[:, :], MUL))
                V.wait()
                v.tensor_tensor(o, o, glo_tmp[:, j], MUL).then_inc(S("glo_d"), 1)
            dve.wait_ge(S("glo_d"), NT)
            v.sem_inc(S("gla_done"), 1)

            def attend(n, j, edge):
                dve.wait_ge(S("q_T"), n + 1)
                v.tensor_copy(qz[64:128, j, 4:8, :].rearrange("p h i -> p (h i)"), bank(6)[64:128, :])\
                    .then_inc(S("q_ev_d"), 1)

                def scores(h):
                    dve.wait_ge(S("sc_mm"), 8 * n + h + 1)
                    if edge or h:
                        dve.wait_ge(S("p_a"), 8 * n + h - 1)
                    hold(v)
                    v.tensor_tensor_reduce(out=sc[:, h % 2, 0:640], in0=banks[h % 2][:, 0:640],
                                           in1=cc("mask")[:, edge * 640:(edge + 1) * 640], scale=HD ** -0.5,
                                           scalar=sink[:, h:h + 1], op0=ADD, op1=MAX,
                                           accum_out=mx[:, h:h + 1]).then_inc(S("sc_d"), 1)

                scores(0)
                for h in range(HEADS):
                    if h + 1 < HEADS:
                        scores(h + 1)
                    dve.wait_ge(S("p_T"), 8 * n + h + 1)
                    v.tensor_copy(prT[:, h % 2, 256:640], bank(5)[:, 0:384]).then_inc(S("pT_d"), 1)
                dve.wait_ge(S("pv_mm"), 8 * n + 8)
                v.reciprocal(rden, rsum[:, j, :]).then_inc(S("rden_d"), 1)
                dve.wait_ge(S("rden_d"), n + 1)
                v.tensor_tensor(mix[:, n, 0:512].rearrange("p (h d) -> p h d", h=HEADS),
                                bank(7).rearrange("p (h d) -> p h d", h=HEADS),
                                wide(rden.unsqueeze(2), [P, HEADS, HD]), MUL).then_inc(S("att_out"), 1)

            dve.wait_ge(S("wa2_in"), 144)
            run_att(dve, attend)

            def ln_stats(norm, t, z):
                j = t % 2
                if t >= 2:
                    dve.wait_ge(S("nrm"), NT * norm + t - 1)
                v.bn_stats(bn6[:, 0, 0:6], z[:, j, 0:512])
                V(v.bn_stats(bn6[:, 0, 6:12], z[:, j, 512:1024]))
                V.wait()
                v.bn_aggr(mv[:, j, :], bn6[:, 0, :]).then_inc(S("var"), 1)

            def ln_scale(norm, t):
                j = t % 2
                dve.wait_ge(S("sd"), NT * norm + t + 1)
                V(v.reciprocal(rs[:, j:j + 1], sd[:, j:j + 1]))
                V.wait()
                v.scalar_tensor_tensor(nm[:, j:j + 1], mv[:, j, 0:1], -1.0, rs[:, j:j + 1], MUL, MUL)\
                    .then_inc(S("nmr"), 1)

            def residual(l, t, z, x):
                j = t % 2
                dve.wait_ge(S("out_mm"), l * NT + t + 1)
                if t >= 2:
                    dve.wait_ge(S("ln"), 2 * l * NT + t - 1)
                V(v.tensor_tensor(z[:, j], banks[j][:, :], gate[:, 0, :], MUL))
                V.wait()
                v.scalar_tensor_tensor(z[:, j], x, ALPHA, z[:, j], MUL, ADD).then_inc(S("res"), 1)
                dve.wait_ge(S("res"), l * NT + t + 1)

            def mixT_half(t):
                dve.wait_ge(S("tile_T"), NTC + t + 1)
                v.tensor_copy(mixT[:, t % 2, 4:8, :].rearrange("p k i -> p (k i)"), bank(5 + 2 * (t % 2)))\
                    .then_inc(S("tile_d"), 1)

            def moe(l):
                for t in range(NT):
                    dve.wait_ge(S("tile_T"), NTC + NT + 2 * NT * l + t + 1)
                    modulated(xT[:, t % 2], 4 + 2 * (t % 2), 2, 0, "tile_d")
                red = v.tensor_reduce
                dve.wait_ge(S("logits"), l + 1)
                V(v.tensor_copy(logit, bank(0)[:, 0:288].rearrange("p (t n) -> p t n", t=NT)))
                V.wait()
                lg, le = logit[:, :, 0:NG], logit[:, :, NG:]

                def first_max(x, best, rank, n, eq, key, kmax, hot):
                    w = wide(best.unsqueeze(2), [P, NT, n])
                    V(v.tensor_tensor(eq, x, w, ALU.is_equal))
                    V.wait()
                    V(v.tensor_tensor(key, eq, wide(cc(rank).unsqueeze(1), [P, NT, n]), MUL))
                    V.wait()
                    V(red(kmax, key, AX.X, MAX))
                    V.wait()
                    V(v.tensor_tensor(hot, key, wide(kmax.unsqueeze(2), [P, NT, n]), ALU.is_equal))
                    V.wait()

                gmax, km, pg, dlt, ex, w0 = rc8[0], rc8[1], rc8[2], rc8[5], rc8[6], rc8[7]
                V(red(gmax, lg, AX.X, MAX))
                V.wait()
                v.tensor_tensor(rs8[0], lg, wide(gmax.unsqueeze(2), [P, NT, NG]), SUB).then_inc(S("gd_d"), 1)
                first_max(lg, gmax, "rank4", NG, rs8[2], rs8[2], km, rs8[3])
                dve.wait_ge(S("route_a"), l * 2 + 1)
                V(red(pg, rs8[1], AX.X, ADD))
                V.wait()
                V(v.reciprocal(pg, pg))
                V(v.tensor_scalar(rs8[2], rs8[3], 1e30, -1e30, MUL, ADD))
                V.wait()
                V(v.tensor_tensor(rt[0].rearrange("p t (g e) -> p t g e", g=NG),
                                  le.rearrange("p t (g e) -> p t g e", g=NG),
                                  wide(rs8[2].unsqueeze(3), [P, NT, NG, NE // NG]), ADD))
                V.wait()
                V(red(rc8[3], rt[0], AX.X, MAX))
                V.wait()
                first_max(rt[0], rc8[3], "rank32", NE, rt[1], rt[1], km, pick[:, 0])
                V(v.scalar_tensor_tensor(rt[2], pick[:, 0], -2e30, rt[0], MUL, ADD))
                V.wait()
                V(red(rc8[4], rt[2], AX.X, MAX))
                V.wait()
                first_max(rt[2], rc8[4], "rank32", NE, rt[1], rt[1], km, pick[:, 1])
                v.tensor_tensor(dlt, rc8[4], rc8[3], SUB).then_inc(S("dlt_d"), 1)
                v.tensor_tensor(chosen.rearrange("p (t e) -> p t e", t=NT), pick[:, 0], pick[:, 1], ADD)\
                    .then_inc(S("chosen"), 1)
                dve.wait_ge(S("route_a"), l * 2 + 2)
                V(v.tensor_scalar(w0, ex, 1.0, None, ADD))
                V.wait()
                V(v.reciprocal(w0, w0))
                V.wait()
                V(v.tensor_tensor(wts[:, 0], w0, pg, MUL))
                V.wait()
                V(v.tensor_tensor(wts[:, 1], wts[:, 0], ex, MUL))
                dve.wait_ge(S("ranked"), l + 1)
                nb, incl, off, cnt = re32[0], re32[1], re32[2], re32[3]
                V(v.tensor_copy(cnt, bank(3)[:, 0:NE]))
                V.wait()
                V(v.tensor_scalar(nb, cnt, float(P), None, ALU.is_gt))
                for m in range(2, SEQ // P):
                    V.wait()
                    V(v.scalar_tensor_tensor(nb, cnt, float(m * P), nb, ALU.is_gt, ADD))
                V.wait()
                V(v.tensor_tensor_scan(incl, cc("ones")[:, 0:NE], nb, 0.0, MUL, ADD))
                V.wait()
                V(v.tensor_tensor(off, incl, nb, SUB))
                V.wait()
                V(v.scalar_tensor_tensor(off, off, float(P), cc("over"), MUL, ADD))
                V.wait()
                rank = bank(2)[:, 0:256].rearrange("p (t e) -> p t e", t=NT)
                V(v.tensor_scalar(rt[3], rank, float(P), None, ALU.is_ge))
                V(v.tensor_tensor(rt[4], rank, wide(cc("first").unsqueeze(1), [P, NT, NE]), ADD))
                V.wait()
                V(v.tensor_tensor(rt[3], rt[3], wide(off.unsqueeze(1), [P, NT, NE]), MUL))
                V.wait()
                V(v.tensor_tensor(rt[4], rt[4], rt[3], ADD))
                V.wait()
                for k in range(2):
                    V(v.tensor_tensor(rt[5 + k], pick[:, k], rt[4], MUL))
                V.wait()
                for k in range(2):
                    V(red(rc8[8 + k], rt[5 + k], AX.X, ADD))
                V.wait()
                for k in range(2):
                    last = v.tensor_copy(dest[:, k * NT:(k + 1) * NT], rc8[8 + k])
                last.then_inc(S("dest"), 1)
                V(v.tensor_tensor(rov[0:1], wide(incl[0:1, :].unsqueeze(1), [1, 16, NE]),
                                  cc("slot")[0:1, :].rearrange("p (o e) -> p o e", e=NE), ALU.is_le))
                V.wait()
                V(red(re32[4][0:1, 0:16], rov[0:1], AX.X, ADD))
                V.wait()
                V(v.tensor_scalar(re32[4][0:1, 0:16], re32[4][0:1, 0:16], float(NE - 1), None, MIN))
                V.wait()
                v.tensor_copy(ov[0:1, 0:16], re32[4][0:1, 0:16])
                v.tensor_copy(ov[0:1, 16:17], incl[0:1, NE - 1:NE]).then_inc(S("routed"), 1)
                dve.wait_ge(S("table_in"), l * 16 + 16)
                v.tensor_scalar(tok, rows_of, 1, None, ALU.arith_shift_right).then_inc(S("tok"), 1)

                def rows_T(i, j):
                    b = 2 * i + j
                    dve.wait_ge(S(f"x_T{l}"), b + 1)
                    modulated(xT[:, j], 2, 2, 0, f"xT_d{l}")

                def gate_up(b):
                    dve.wait_ge(S(f"silu_a{l}"), b + 2)
                    dve.wait_ge(S(f"h_mm{l}"), 2 * b + 2)
                    v.tensor_tensor(gg, sg, bank(1), MUL).then_inc(S(f"g_d{l}"), 1)

                def gated(b):
                    dve.wait_ge(S(f"g_T{l}"), b + 1)
                    v.tensor_copy(gT[:, 2:4, :].rearrange("p k i -> p (k i)"), bank(5)[:, 0:256])\
                        .then_inc(S(f"gT_d{l}"), 1)

                def output(b, j):
                    dve.wait_ge(S(f"y_mm{l}"), b + 1)
                    dve.wait_ge(S(f"yo_free{l}"), b + 1)
                    v.tensor_copy(yo[:, j, 512:1024], bank(7)).then_inc(S(f"y_d{l}"), 1)

                def hidden(i, j, after):
                    b = 2 * i + j
                    if after:
                        gated(b - 1)
                    gate_up(b)
                    rows_T(i + j, 1 - j)
                    if after:
                        output(b - 1, 1 - j)

                def product(i, j):
                    gated(2 * i + j)
                    output(2 * i + j, j)

                def block_of(i, j):
                    gate_up(2 * i + j)
                    rows_T(i + j, 1 - j)
                    product(i, j)

                rows_T(0, 0)
                v.sem_inc(S(f"y_d{l}"), 1)
                v.sem_inc(S(f"g_d{l}"), 1)
                run_blocks(dve, l, hidden, product, block_of)
                if l == 0:
                    cond_rows(1)
                for t in range(NT):
                    j = t % 2
                    dve.wait_ge(S(f"pair_in{j}"), 16 * (NT // 2 * l + t // 2 + 1))
                    if t >= 2:
                        dve.wait_ge(S("ln"), (2 * l + 1) * NT + t - 1)
                    z = zt[:, j]
                    V(v.tensor_scalar(z, pair[:, j, 0, :], wts[:, 0, t:t + 1], None, MUL))
                    V.wait()
                    V(v.scalar_tensor_tensor(z, pair[:, j, 1, :], wts[:, 1, t:t + 1], z, MUL, ADD))
                    V.wait()
                    V(v.tensor_tensor(z, z, gate[:, 1, :], MUL))
                    V.wait()
                    v.scalar_tensor_tensor(z, hh[:, t], ALPHA, z, MUL, ADD).then_inc(S("comb"), 1)
                    dve.wait_ge(S("comb"), l * NT + t + 1)
                    ln_stats(2 * l + 1, t, zt)
                    ln_scale(2 * l + 1, t)

            for t in range(NT):
                mixT_half(t)
                if t:
                    dve.wait_ge(S(f"x_in{(t - 1) % 2}"), 16 * ((t - 1) // 2 + 5 - (t - 1) % 2))
                    residual(0, t - 1, zt, xin[:, (t - 1) % 2])
                    ln_stats(0, t - 1, zt)
                    ln_scale(0, t - 1)
            dve.wait_ge(S("x_in1"), 16 * (NT // 2 + 3))
            residual(0, NT - 1, zt, xin[:, 1])
            ln_stats(0, NT - 1, zt)
            ln_scale(0, NT - 1)
            moe(0)
            mod_columns(1)
            for t in range(NT):
                dve.wait_ge(S("tile_T"), NTC + 2 * NT + t + 1)
                modulated(u1T[:, :, t * P:(t + 1) * P], 4 + 2 * (t % 2), 0, 0, "tile_d")
            dve.wait_ge(S("wa2_in"), 144)
            for j in range(2):
                v.memset(conv_in[:, j, 0:1], 0.0)
                V(v.memset(conv_in[:, j, SEQ + 1:SEQ + 2], 0.0))
            V.wait()
            v.sem_inc(S("conv_d"), 2)
            v.sem_inc(S("z_ok"), 2)
            with dve.Fori(0, KC // 2) as i:
                for j in range(2):
                    c = 2 * i + j
                    for half in range(2):
                        dve.wait_ge(S("conv_a"), 2 * c + half + 3)
                        v.tensor_tensor(conv_in[:, j, 1 + half * 512:513 + half * 512], bank(3 * half + 2),
                                        conv_u[:, half], MUL).then_inc(S("conv_d"), 1)
                    dve.wait_ge(S("conv_d"), 2 * c + 4)

                    def par(m):
                        return convp[:, m, bass.ds(c, 1)]

                    v.tensor_scalar(conv_y, conv_in[:, j, 0:SEQ], par(0), None, MUL).then_inc(S("taps"), 1)
                    dve.wait_ge(S("taps"), 3 * c + 1)
                    v.scalar_tensor_tensor(conv_y, conv_in[:, j, 1:SEQ + 1], par(1), conv_y, MUL, ADD).then_inc(S("taps"), 1)
                    dve.wait_ge(S("taps"), 3 * c + 2)
                    v.scalar_tensor_tensor(conv_y, conv_in[:, j, 2:SEQ + 2], par(2), conv_y, MUL, ADD).then_inc(S("taps"), 1)
                    dve.wait_ge(S("taps"), 3 * c + 3)
                    v.scalar_tensor_tensor(zT[:, c, :], conv_y, par(3), conv_b2[:, j], ADD, MUL).then_inc(S("z_ok"), 1)
            for t in range(NT):
                residual(1, t, zt1, hh[:, t])
                ln_stats(2, t, zt1)
                ln_scale(2, t)
            moe(1)

        @block.gpsimd
        def _(pool):
            G = Steps(pool, "pool_step")
            pool.wait_ge(S("proj_mm"), len(units))
            pool.memset(lowT[32:33, :, :], 1.0).then_inc(S("k_pad"), 1)
            pool.wait_ge(S("k_pad"), 1)
            pool.memset(kT[:, 0:P], 0.0).then_inc(S("k_pad"), 1)
            pool.memset(kT[:, 1152:1280], 0.0).then_inc(S("k_pad"), 1)
            pool.wait_ge(S("gate_d"), NTC)

            def gla(n, m, q, ts, add):
                for s in range(2):
                    pool.wait_ge(S("g_cum"), 2 * n)
                    hold(pool)
                    pool.tensor_copy(logs[:, s, :], gates_log[:, ts[s], s * 256:(s + 1) * 256]).then_inc(S("g_log"), 1)

            run_gla(pool, gla)
            pool.wait_ge(S("gla_done"), 1)
            for j in range(2):
                pool.memset(qz[64:128, j, 0:4, :], 0.0).then_inc(S("qz_zero"), 1)
                pool.wait_ge(S("qz_zero"), 2 * j + 1)
                pool.memset(qz[0:64, j, 4:8, :], 0.0).then_inc(S("qz_zero"), 1)
                pool.wait_ge(S("qz_zero"), 2 * j + 2)
            pool.wait_ge(S("wa2_in"), 144)

            def attend(n, j, edge):
                pool.wait_ge(S("q_T"), n)
                hold(pool)
                pool.tensor_copy(qrow[:, j].rearrange("p (r g d) -> p r g d", r=4, g=2),
                                 proj[:, n, Q0:Q0 + 512].rearrange("p (g r d) -> p r g d", g=2, r=4))\
                    .then_inc(S("q_row"), 1)
                for h in range(HEADS):
                    if edge or h:
                        pool.wait_ge(S("p_a"), 8 * n + h - 1)
                        hold(pool)
                    pool.tensor_copy(sc[:, h % 2, 640:641], sink[:, h:h + 1]).then_inc(S("sink_c"), 1)

            run_att(pool, attend)

            def ln(l, k, t, z):
                j, n = t % 2, NT * (2 * l + k) + t
                if t == 0:
                    pool.wait_ge(S("ln_in"), 32 * (2 * l + k + 1))
                pool.wait_ge(S("nrm"), n + 1)
                G(pool.tensor_tensor(z[:, j], z[:, j], lnw, MUL))
                G.wait()
                pool.tensor_tensor(hh[:, t], z[:, j], lnb, ADD).then_inc(S("ln"), 1)

            def moe(l):
                pool.wait_ge(S("cond_in"), 80)
                pool.wait_ge(S("dest"), l + 1)
                for c in range(16):
                    pool.indirect_dma_start(out=t_dram[l], out_offset=bass.IndirectOffsetOnAxis(ap=dest[:, c:c + 1], axis=0),
                                            in_=rownum[:, c:c + 1], in_offset=None, bounds_check=TABLE * P - 1,
                                            oob_is_err=False).then_inc(S("placed"), 16)
                pool.wait_ge(S("placed"), l * 256 + 16 * 16)
                pool.dma_start(rows_of, t_dram[l].rearrange("(b p) o -> p (b o)", p=P),
                               allow_slow_non_contiguous=True).then_inc(S("table_in"), 16)
                for j in range(2):
                    G(pool.memset(xg[:, j], 0.0))
                G.wait()
                pool.wait_ge(S("tok"), l + 1)
                pool.wait_ge(S("h_out"), l * 16 * NT + 16 * NT)

                def gather(i, j, copies):
                    pool.tensor_copy(gidx[:, j:j + 1], tok[:, bass.ds(2 * i + j, 1)]).then_inc(S(f"row_idx{l}"), 1)
                    pool.wait_ge(S(f"row_idx{l}"), copies)
                    hold(pool)
                    pool.indirect_dma_start(out=xg[:, j], out_offset=None, in_=h_dram[l],
                                            in_offset=bass.IndirectOffsetOnAxis(ap=gidx[:, j:j + 1], axis=0),
                                            bounds_check=SEQ - 1, oob_is_err=False).then_inc(S(f"xg_in{l}_{j}"), 16)

                gather(0, 0, 1)
                gather(0, 1, 2)
                for j in range(2):
                    pool.wait_ge(S(f"xg_in{l}_{j}"), 16)
                pool.wait_ge(S(f"x_T{l}"), 1)
                gather(1, 0, 3)
                pool.wait_ge(S(f"xg_in{l}_0"), 32)
                pool.sem_inc(S(f"yo_free{l}"), 2)

                def block_of(i, j):
                    b = 2 * i + j
                    pool.tensor_copy(sidx[:, j:j + 1], rows_of[:, bass.ds(b, 1)]).then_inc(S(f"row_idx{l}"), 1)
                    pool.wait_ge(S(f"x_T{l}"), b + 2)
                    gather(i + j + 1, 1 - j, 2 * b + 5)
                    pool.wait_ge(S(f"row_idx{l}"), 2 * b + 4)
                    pool.wait_ge(S(f"y_a{l}"), b + 2)
                    pool.wait_ge(S(f"y_d{l}"), b + 2)
                    hold(pool)
                    pool.indirect_dma_start(out=y_dram[l], out_offset=bass.IndirectOffsetOnAxis(ap=sidx[:, j:j + 1], axis=0),
                                            in_=yo[:, j], in_offset=None, bounds_check=ROWS - 1,
                                            oob_is_err=False).then_inc(S(f"y_out{l}"), 16)
                    pool.wait_ge(S(f"xg_in{l}_{1 - j}"), 16 * (i + j + 2))
                    pool.wait_ge(S(f"y_out{l}"), 16 * (b + 1))
                    pool.sem_inc(S(f"yo_free{l}"), 1)

                block_of(0, 0)
                with pool.Fori(0, NE // 2 - 1) as i:
                    block_of(i, 1)
                    block_of(i + 1, 0)
                block_of(NE // 2 - 1, 1)
                run_over(pool, l, block_of)
                pool.sem_inc(S("rows_out"), 1)
                for t in range(NT):
                    ln(l, 1, t, zt)

            for t in range(NT):
                ln(0, 0, t, zt)
            moe(0)
            for t in range(NT):
                ln(1, 0, t, zt1)
            moe(1)


GLA_SCALE = 64 ** -0.5

_INS = ["x", "c", "ctx", "c_ctx", "w_in_even", "w_out_even", "attn_sink", "gla_wa2", "gla_ba", "gla_norm_w", "w_in_odd",
        "conv_w", "conv_b", "w_out_odd", "ada_w", "ada_b", "ln_w", "ln_b", "router_wg", "router_bg", "router_we",
        "router_be", "moe_w1", "moe_w3", "moe_w2"]


def kernel(**inputs):
    import concourse.bacc as _bacc
    from concourse.bass_utils import run_bass_kernel_spmd as _run

    nc = _bacc.Bacc("TRN2", target_bir_lowering=False, num_devices=1)
    arrays, T = {}, {}
    tables = {"const_f": constants(), "const_i": row_numbers(), "const_t": np.full((TABLE * P, 1), ROWS, np.int32)}
    for name in _INS + list(tables):
        a = np.ascontiguousarray(inputs[name] if name in inputs else tables[name])
        arrays[f"in_{name}"] = a
        T[name] = nc.dram_tensor(f"in_{name}", a.shape, mybir.dt.from_np(a.dtype), kind="ExternalInput").ap()
    out = nc.dram_tensor("out_0", (1, SEQ, D), mybir.dt.float32, kind="ExternalOutput").ap()
    program(nc, T, out)
    r = _run(nc, [arrays], core_ids=[0])
    return r.results[0]["out_0"]
```
